# Optimizing a Trainium2 kernel written in Bass

```python
import jax, jax.numpy as jnp
from jax import lax
import numpy as np

D_MODEL = 1024
BATCH = 1
SEQ = 256
DEPTH = 2

CHUNK = 64
HEAD_DIM = 64
ROPE_THETA = 10000.0
NORM_EPS = 1e-6

A_GROUPS = 4
A_WIDTH = A_GROUPS * HEAD_DIM
A_BLOCK = 128

B_Q_HEADS = 8
B_KV_HEADS = 2
B_WINDOW = 128
B_WIN_CHUNKS = B_WINDOW // CHUNK

C_HEADS = 4
C_LATENT = 128
C_IDX_HEADS = 4
C_IDX_DIM = 64
C_TOPK_MAX = 256
C_Q_BLOCK = 128

D_GROUPS = 4
D_GROUP_DIM = 64
D_WIDTH = D_GROUPS * D_GROUP_DIM
D_POOL_SIZES = (2, 4, 8, 16)

N_BRANCH = 4
FFN_HIDDEN = ((-(-8 * D_MODEL // 3) + 255) // 256) * 256

IN_SIZES = (
    2 * A_WIDTH,
    B_Q_HEADS * HEAD_DIM,
    B_KV_HEADS * HEAD_DIM,
    B_KV_HEADS * HEAD_DIM,
    C_HEADS * HEAD_DIM,
    C_LATENT,
    C_IDX_HEADS * C_IDX_DIM,
    C_IDX_DIM,
    C_IDX_HEADS,
    D_WIDTH,
    N_BRANCH * D_MODEL,
)
IN_WIDTH = int(sum(IN_SIZES))

kernel_name = 'hybrid_gated_streaming_block'

def _split(t, sizes):
    idx = np.cumsum(sizes)[:-1].tolist()
    return jnp.split(t, idx, axis=-1)

def _rms_norm(x, g):
    xf = x.astype(jnp.float32)
    y = xf * lax.rsqrt(jnp.mean(xf * xf, axis=-1, keepdims=True) + NORM_EPS)
    return (y * g.astype(jnp.float32)).astype(x.dtype)

def _rope_tables(positions):
    inv_freq = ROPE_THETA ** (-jnp.arange(0, HEAD_DIM, 2, dtype=jnp.float32) / HEAD_DIM)
    ang = positions.astype(jnp.float32)[..., None] * inv_freq
    return jnp.cos(ang), jnp.sin(ang)

def _apply_rope(x, cos, sin):
    half = x.shape[-1] // 2
    xf = x.astype(jnp.float32)
    c = cos[:, :, None, :]
    s = sin[:, :, None, :]
    x1, x2 = xf[..., :half], xf[..., half:]
    return jnp.concatenate([x1 * c - x2 * s, x2 * c + x1 * s], axis=-1).astype(x.dtype)

def _gmlp_mixer(za, v_gain, w_spatial, b_spatial):
    Bsz, S, _ = za.shape
    u, v = jnp.split(za, 2, axis=-1)
    v = _rms_norm(v, v_gain)
    vb = v.reshape(Bsz, S // A_BLOCK, A_BLOCK, A_GROUPS, HEAD_DIM)
    i = np.arange(A_BLOCK)
    mask = (i[:, None] // CHUNK >= i[None, :] // CHUNK).astype(np.float32)
    w = w_spatial * jnp.asarray(mask, dtype=w_spatial.dtype)
    s = jnp.einsum('gij,bnjgc->bnigc', w, vb) + b_spatial.T[None, None, :, :, None]
    return u * s.reshape(Bsz, S, A_WIDTH)

def _swa_sink_mixer(q, k, v, q_gain, k_gain, sinks, cos, sin):
    Bsz, S = q.shape[:2]
    dt = q.dtype
    n_chunks = S // CHUNK
    groups = B_Q_HEADS // B_KV_HEADS
    q = _apply_rope(_rms_norm(q, q_gain), cos, sin)
    k = _apply_rope(_rms_norm(k, k_gain), cos, sin)
    qc = q.reshape(Bsz, n_chunks, CHUNK, B_KV_HEADS, groups, HEAD_DIM)
    kc = k.reshape(Bsz, n_chunks, CHUNK, B_KV_HEADS, HEAD_DIM)
    vc = v.reshape(Bsz, n_chunks, CHUNK, B_KV_HEADS, HEAD_DIM)
    offsets = list(range(B_WIN_CHUNKS - 1, -1, -1))

    def band(t):
        parts = [jnp.pad(t, ((0, 0), (o, 0), (0, 0), (0, 0), (0, 0)))[:, :n_chunks] for o in offsets]
        return jnp.concatenate(parts, axis=2)

    kb, vb = band(kc), band(vc)
    slot_off = np.repeat(np.array(offsets), CHUNK)
    valid = jnp.asarray(np.arange(n_chunks)[:, None] >= slot_off[None, :])
    scores = jnp.einsum('bcqhgd,bckhd->bchgqk', qc, kb).astype(jnp.float32) * (HEAD_DIM ** -0.5)
    scores = jnp.where(valid[None, :, None, None, None, :], scores, -jnp.inf)
    sink = sinks.astype(jnp.float32).reshape(B_KV_HEADS, groups)[None, None, :, :, None, None]
    m = jnp.maximum(jnp.max(scores, axis=-1, keepdims=True), sink)
    p = jnp.exp(scores - m)
    probs = (p / (jnp.sum(p, axis=-1, keepdims=True) + jnp.exp(sink - m))).astype(dt)
    out = jnp.einsum('bchgqk,bckhd->bcqhgd', probs, vb)
    return out.reshape(Bsz, S, B_Q_HEADS * HEAD_DIM)

def _dsa_mixer(q, latent, qi, ki, wi, q_gain, k_gain, latent_gain, w_uk, w_uv, cos, sin):
    Bsz, S = q.shape[:2]
    dt = q.dtype
    lat = _rms_norm(latent, latent_gain)
    k = jnp.einsum('bsl,ld->bsd', lat, w_uk)
    v = jnp.einsum('bsl,ld->bsd', lat, w_uv)
    q = _apply_rope(_rms_norm(q, q_gain), cos, sin)
    k = _apply_rope(_rms_norm(k, k_gain)[:, :, None, :], cos, sin)[:, :, 0, :]
    qi = _apply_rope(qi, cos, sin)
    ki = _apply_rope(ki[:, :, None, :], cos, sin)[:, :, 0, :]
    wi = wi * (C_IDX_HEADS ** -0.5)
    topk = min(C_TOPK_MAX, S // 4)
    n_blocks = S // C_Q_BLOCK
    key_chunk = jnp.arange(S) // CHUNK
    idx_scale = C_IDX_DIM ** -0.5
    attn_scale = HEAD_DIM ** -0.5

    def to_blocks(t):
        return jnp.swapaxes(t.reshape((Bsz, n_blocks, C_Q_BLOCK) + t.shape[2:]), 0, 1)

    def one_block(args):
        qb, qib, wib, blk = args
        t_chunk = (blk * C_Q_BLOCK + jnp.arange(C_Q_BLOCK)) // CHUNK
        adm = key_chunk[None, :] <= t_chunk[:, None]
        dots = jnp.einsum('bqhd,bsd->bhqs', qib, ki).astype(jnp.float32) * idx_scale
        score = jnp.einsum('bqh,bhqs->bqs', wib.astype(jnp.float32), jax.nn.relu(dots))
        score = jnp.where(adm[None], score, -jnp.inf)
        _, idx = lax.top_k(score, topk)
        valid = key_chunk[idx] <= t_chunk[None, :, None]
        kg = jax.vmap(lambda kk, ii: kk[ii])(k, idx)
        vg = jax.vmap(lambda vv, ii: vv[ii])(v, idx)
        logits = jnp.einsum('bqhd,bqkd->bhqk', qb, kg).astype(jnp.float32) * attn_scale
        logits = jnp.where(valid[:, None], logits, -jnp.inf)
        probs = jax.nn.softmax(logits, axis=-1).astype(dt)
        return jnp.einsum('bhqk,bqkd->bqhd', probs, vg)

    blk_ids = jnp.arange(n_blocks, dtype=jnp.int32)
    out = lax.map(one_block, (to_blocks(q), to_blocks(qi), to_blocks(wi), blk_ids))
    return jnp.swapaxes(out, 0, 1).reshape(Bsz, S, C_HEADS * HEAD_DIM)

def _pool_mixer(xd, w_group, scale):
    Bsz, S, _ = xd.shape
    xf = xd.astype(jnp.float32)
    cs = jnp.pad(jnp.cumsum(xf, axis=1), ((0, 0), (1, 0), (0, 0)))
    t = jnp.arange(S)
    pooled = []
    for g, w in enumerate(D_POOL_SIZES):
        csg = cs[..., g * D_GROUP_DIM:(g + 1) * D_GROUP_DIM]
        lo = jnp.maximum(t + 1 - w, 0)
        win_sum = csg[:, 1:] - jnp.take(csg, lo, axis=1)
        cnt = jnp.minimum(t + 1, w).astype(jnp.float32)[None, :, None]
        pooled.append(win_sum / cnt)
    pooled = jnp.stack(pooled, axis=2)
    mixed = (pooled - xf.reshape(Bsz, S, D_GROUPS, D_GROUP_DIM)).astype(xd.dtype)
    y = jnp.einsum('bsgc,gcd->bsgd', mixed, w_group).reshape(Bsz, S, D_WIDTH)
    return y * scale

def _hybrid_layer(x, cos, sin, norm_mix, w_in, a_v_gain, a_w_spatial, a_b_spatial, a_w_out,
                  b_q_gain, b_k_gain, b_sinks, b_w_out, c_q_gain, c_k_gain, c_latent_gain,
                  c_w_uk, c_w_uv, c_w_out, d_w_group, d_scale, d_w_out, w_o, norm_ffn,
                  w_gate_up, w_down):
    Bsz, S, _ = x.shape
    h = _rms_norm(x, norm_mix)
    z = jnp.einsum('bsd,de->bse', h, w_in)
    za, bq, bk, bv, cq, clat, ciq, cik, ciw, zd, zg = _split(z, IN_SIZES)
    ya = _gmlp_mixer(jax.nn.gelu(za), a_v_gain, a_w_spatial, a_b_spatial)
    yb = _swa_sink_mixer(bq.reshape(Bsz, S, B_Q_HEADS, HEAD_DIM),
                         bk.reshape(Bsz, S, B_KV_HEADS, HEAD_DIM),
                         bv.reshape(Bsz, S, B_KV_HEADS, HEAD_DIM),
                         b_q_gain, b_k_gain, b_sinks, cos, sin)
    yc = _dsa_mixer(cq.reshape(Bsz, S, C_HEADS, HEAD_DIM), clat,
                    ciq.reshape(Bsz, S, C_IDX_HEADS, C_IDX_DIM), cik, ciw,
                    c_q_gain, c_k_gain, c_latent_gain, c_w_uk, c_w_uv, cos, sin)
    yd = _pool_mixer(zd, d_w_group, d_scale)
    gates = jax.nn.sigmoid(zg).reshape(Bsz, S, N_BRANCH, D_MODEL)
    merged = (gates[:, :, 0] * (ya @ a_w_out) + gates[:, :, 1] * (yb @ b_w_out)
              + gates[:, :, 2] * (yc @ c_w_out) + gates[:, :, 3] * (yd @ d_w_out))
    x = x + merged @ w_o
    h2 = _rms_norm(x, norm_ffn)
    gate, up = jnp.split(h2 @ w_gate_up, 2, axis=-1)
    return x + (jax.nn.silu(gate) * up) @ w_down

def setup_inputs(seed: int = 0) -> dict:
    key = jax.random.key(seed)
    ks = jax.random.split(key, 32)
    f32 = jnp.float32

    def nrm(k, shape, scale):
        return jax.random.normal(k, shape, f32) * scale

    def gain(k, shape):
        return 1.0 + 0.02 * jax.random.normal(k, shape, f32)

    L = DEPTH
    x = jax.random.normal(ks[0], (BATCH, SEQ, D_MODEL), f32)
    offset = jax.random.randint(ks[1], (BATCH, 1), 0, 1024, dtype=jnp.int32)
    positions = (offset + jnp.arange(SEQ, dtype=jnp.int32)[None, :]).astype(jnp.int32)
    return {
        'x': x,
        'positions': positions,
        'norm_mix': gain(ks[2], (L, D_MODEL)),
        'w_in': nrm(ks[3], (L, D_MODEL, IN_WIDTH), D_MODEL ** -0.5),
        'a_v_gain': gain(ks[4], (L, A_WIDTH)),
        'a_w_spatial': nrm(ks[5], (L, A_GROUPS, A_BLOCK, A_BLOCK), A_BLOCK ** -0.5),
        'a_b_spatial': gain(ks[6], (L, A_GROUPS, A_BLOCK)),
        'a_w_out': nrm(ks[7], (L, A_WIDTH, D_MODEL), A_WIDTH ** -0.5),
        'b_q_gain': gain(ks[8], (L, HEAD_DIM)),
        'b_k_gain': gain(ks[9], (L, HEAD_DIM)),
        'b_sinks': nrm(ks[10], (L, B_Q_HEADS), 0.5),
        'b_w_out': nrm(ks[11], (L, B_Q_HEADS * HEAD_DIM, D_MODEL), (B_Q_HEADS * HEAD_DIM) ** -0.5),
        'c_q_gain': gain(ks[12], (L, HEAD_DIM)),
        'c_k_gain': gain(ks[13], (L, HEAD_DIM)),
        'c_latent_gain': gain(ks[14], (L, C_LATENT)),
        'c_w_uk': nrm(ks[15], (L, C_LATENT, HEAD_DIM), C_LATENT ** -0.5),
        'c_w_uv': nrm(ks[16], (L, C_LATENT, HEAD_DIM), C_LATENT ** -0.5),
        'c_w_out': nrm(ks[17], (L, C_HEADS * HEAD_DIM, D_MODEL), (C_HEADS * HEAD_DIM) ** -0.5),
        'd_w_group': nrm(ks[18], (L, D_GROUPS, D_GROUP_DIM, D_GROUP_DIM), D_GROUP_DIM ** -0.5),
        'd_scale': 1.0 + 0.1 * jax.random.normal(ks[19], (L, D_WIDTH), f32),
        'd_w_out': nrm(ks[20], (L, D_WIDTH, D_MODEL), D_WIDTH ** -0.5),
        'w_o': nrm(ks[21], (L, D_MODEL, D_MODEL), D_MODEL ** -0.5),
        'norm_ffn': gain(ks[22], (L, D_MODEL)),
        'w_gate_up': nrm(ks[23], (L, D_MODEL, 2 * FFN_HIDDEN), D_MODEL ** -0.5),
        'w_down': nrm(ks[24], (L, FFN_HIDDEN, D_MODEL), FFN_HIDDEN ** -0.5),
    }

def reference(x, positions, norm_mix, w_in, a_v_gain, a_w_spatial, a_b_spatial, a_w_out,
              b_q_gain, b_k_gain, b_sinks, b_w_out, c_q_gain, c_k_gain, c_latent_gain,
              c_w_uk, c_w_uv, c_w_out, d_w_group, d_scale, d_w_out, w_o, norm_ffn,
              w_gate_up, w_down):
    cos, sin = _rope_tables(positions)
    for l in range(DEPTH):
        x = _hybrid_layer(x, cos, sin, norm_mix[l], w_in[l], a_v_gain[l], a_w_spatial[l],
                          a_b_spatial[l], a_w_out[l], b_q_gain[l], b_k_gain[l], b_sinks[l],
                          b_w_out[l], c_q_gain[l], c_k_gain[l], c_latent_gain[l], c_w_uk[l],
                          c_w_uv[l], c_w_out[l], d_w_group[l], d_scale[l], d_w_out[l], w_o[l],
                          norm_ffn[l], w_gate_up[l], w_down[l])
    return x


_drawn_inputs = setup_inputs


def setup_inputs(seed=0):
    import zlib

    import numpy as np

    out = dict(_drawn_inputs(seed))
    spreads = {}
    factors = {'a_v_gain': 5.574,
     'a_b_spatial': 5.208,
     'b_q_gain': 8.0,
     'b_k_gain': 8.0,
     'b_sinks': 8.0,
     'c_q_gain': 8.0,
     'c_k_gain': 8.0,
     'c_latent_gain': 8.0,
     'norm_ffn': 2.856}
    for name, (base, spread) in spreads.items():
        noise = np.random.default_rng([zlib.crc32(name.encode()), seed]).standard_normal(out[name].shape)
        drawn = base * np.exp(spread * noise) if base else spread * noise
        out[name] = __import__('jax').numpy.asarray(drawn.astype(out[name].dtype))
    for name, factor in factors.items():
        out[name] = (out[name] * factor).astype(out[name].dtype)
    return out
```

```python
from contextlib import ExitStack

import numpy as np

import concourse.bass as bass
from concourse import mybir

F32 = mybir.dt.float32
F32R = mybir.dt.float32r
I32 = mybir.dt.int32
ALU = mybir.AluOpType
ACT = mybir.ActivationFunctionType
AX_X = mybir.AxisListType.X

P = 128
D_MODEL = 1024
SEQ = 256
DEPTH = 2
CHUNK = 64
HD = 64
ROPE_THETA = 10000.0
EPS = 1e-6
A_GROUPS = 4
A_WIDTH = A_GROUPS * HD
TOPK = SEQ // 4
D_POOLS = (2, 4, 8, 16)
FFN = 2816
TB = SEQ // P
KT = D_MODEL // P

C_ZA, C_BQ, C_BK, C_BV, C_CQ, C_LAT, C_IQ, C_IK, C_IW, C_ZD, C_ZG = (
    0, 512, 1024, 1152, 1280, 1536, 1664, 1920, 1984, 1988, 2244)
IN_WIDTH = C_ZG + 4 * D_MODEL

N = 512
PIECES = 4
FC = 256
NF = FFN // FC
SCALE = HD ** -0.5
NEG = -1e30
OUTSIDE = -2e38
TAKEN = -3e38
GELU_C = 0.7978845608028654
GELU_A = 0.044715

PROJ = [("idx", C_LAT, C_ZD - C_LAT), ("kv", C_BK, N), ("bq", C_BQ, N), ("za", C_ZA, N), ("zd", C_ZD, 256)]
BRANCHES = ["A", "D", "B", "C"]
BRANCH_ID = {"A": 0, "B": 1, "C": 2, "D": 3}
OUT_K = {"A": 2, "B": 4, "C": 2, "D": 2}


def plan_units():
    units, first = [], {}

    def add(key, parts):
        first[key] = len(units)
        units.extend(parts)

    for j, (name, _, _) in enumerate(PROJ):
        add(("proj", name), [("in", PROJ[j][1], PROJ[j][2], h) for h in range(2)])
    for b in BRANCHES:
        for c in range(2):
            col = C_ZG + BRANCH_ID[b] * D_MODEL + c * N
            add(("gate", b, c), [("in", col, N, h) for h in range(2)])
        if OUT_K[b] == 2:
            add(("out", b), [("out2", b, 0, 0)])
        else:
            for c in range(2):
                add(("out", b, c), [("out4", b, c, 0)])
    for c in range(2):
        add(("wo", c), [("wo", c, 0, h) for h in range(2)])
    for f in range(NF):
        add(("gu", f), [("gu", f, 0, h) for h in range(2)])
        if f >= 2:
            add(("dn", f - 2), [("dn", f - 2, 0, 0)])
    for f in (NF - 2, NF - 1):
        add(("dn", f), [("dn", f, 0, 0)])
    return units, first


UNITS, FIRST = plan_units()
NU = len(UNITS)
RAW = 2
SPLIT = 4
assert NU % RAW == 0 and NU % SPLIT == 0
POOL_UNITS = [0, 1] + list(range(7, 31, 2))
DVE_UNITS = [u for u in range(NU) if u not in POOL_UNITS]


def dmas_of(unit):
    return 2 if unit[0] == "gu" else 1


ATTN = [("B", 0, 0), ("B", 0, 1), ("B", 1, 0), ("B", 1, 1), ("C", 0, 0), ("C", 0, 1)]


def main_uses():
    uses, pair = [], 0

    def chunk(name):
        nonlocal pair
        for tb in range(TB):
            uses.append(((*name, tb), 2 * pair + tb))
        pair = 1 - pair

    for name, _, _ in PROJ:
        chunk(("proj", name))
    for b in BRANCHES:
        for c in range(2):
            chunk(("gate", b, c))
        for c in range(2):
            chunk(("out", b, c))
    for c in range(2):
        chunk(("wo", c))
    for c in range(2):
        chunk(("dn", c))
    return uses


PE_AT = {"wT": 3, "latT": 4, "TI": 5, "kv": 6, "idx0": 7, "TK": 8, "idx1": 9, "TQ": 11, "TC": 11,
         "spatial": 12, "mixed": 12, "yaT": 13, "ydT": 14}
S_AT = [13 + 2 * i for i in range(len(ATTN))]
T_AT = [15 + 2 * i for i in range(len(ATTN))]
Y_AT = [16 + 2 * i for i in range(len(ATTN))]


def mixer_uses():
    def turned(stage):
        return [((stage, tb, h), (2 + h) if tb == 0 else h) for tb in range(TB) for h in range(2)]

    uses = turned("hT")
    uses += [(("wT",), 0), (("latT",), 1), (("TI", 0), 2), (("TI", 1), 3), (("kv",), 0),
             (("idx", 0, 0), 0), (("idx", 0, 1), 1), (("TK", 0), 2), (("TK", 1), 3), (("idx", 1, 0), 0), (("idx", 1, 1), 1),
             (("TQ", 0), 2), (("TQ", 1), 3), (("TC",), 0), (("spatial",), 1), (("mixed",), 2),
             (("yaT",), 3), (("S", 0, 0), 0), (("S", 0, 1), 1), (("ydT", 0), 1), (("ydT", 1), 3)]
    for i, (_, _, tb) in enumerate(ATTN):
        if i + 1 < len(ATTN):
            for k in range(2):
                uses.append((("S", i + 1, k), k))
        for k in range(tb + 1):
            uses.append((("T", i, k), 2 + k))
        uses.append((("Y", i), 2))
    uses += turned("mT") + turned("h2T")
    for f in range(NF):
        for tb in range(TB):
            uses.append((("gu", f, tb), 2 * ((f + 1) % 2) + tb))
            uses.append((("hid", f, tb), 2 * ((f + 1) % 2) + tb))
    return uses


def numbered(uses):
    per, at = [0] * 4, {}
    for name, bank in uses:
        at[name] = (bank, per[bank])
        per[bank] += 1
    return at, per


MAIN, MAIN_PER = numbered(main_uses())
MIX, MIX_PER = numbered(mixer_uses())

NORMS = ["mix", "lat", "K0", "K1", "Q0", "Q1", "ck", "v", "ffn"]
POWER_BEFORE = {"mix": 7, "lat": 7, "K0": 7, "K1": 9, "Q0": 9, "Q1": 11, "ck": 11, "v": 13, "ffn": None}
NORM_WIDTH = {n: {"K": 6, "Q": 8}.get(n[0], 2) for n in NORMS}
N_PARAMS = 15
POOL_CONSTS = 2 + HD // 2 + 1 + 6 * len(D_POOLS) + sum(w - 1 for w in D_POOLS)
TWO_PI = (6.28125, 0.0019350051879882812, 3.019916050561733e-07)
ROUNDER = 1.5 * 2 ** 23
DVE_ANGLES = 8 + 2 * (3 + len(TWO_PI) + 2)
DVE_CONSTS = DVE_ANGLES + 2 + 2 * len(D_POOLS)
TOPK_AT = {14: (0, 0, 4), 16: (0, 4, 8), 18: (1, 0, 4), 20: (1, 4, 8)}
DVE_STEPS = 123


class Signal:

    def __init__(self, sem, per_layer, early=0):
        self.sem, self.per_layer, self.early = sem, per_layer, early

    def nth(self, l, n):
        return self.sem, l * self.per_layer + (n + self.early)


def trunk_kernel(nc, x, positions, norm_mix, w_in, a_v_gain, a_w_spatial, a_b_spatial, a_w_out,
                 b_q_gain, b_k_gain, b_sinks, b_w_out, c_q_gain, c_k_gain, c_latent_gain,
                 c_w_uk, c_w_uv, c_w_out, d_w_group, d_scale, d_w_out, w_o, norm_ffn,
                 w_gate_up, w_down, out):
    w_out = {"A": a_w_out, "B": b_w_out, "C": c_w_out, "D": d_w_out}
    with ExitStack() as ctx:
        def sb(name, shape, dt=F32):
            return ctx.enter_context(nc.sbuf_tensor(name, shape, dt))

        def sem(name):
            return ctx.enter_context(nc.semaphore(name))

        def signal(name, per_layer, credit=0):
            return Signal(sem(name), per_layer, credit)

        raw = sb("raw", [P, RAW, PIECES, N])
        w_hi = sb("w_hi", [P, SPLIT, PIECES, N], F32R)
        w_lo = sb("w_lo", [P, SPLIT, PIECES, N], F32R)
        xs = sb("xs", [P, TB, D_MODEL])
        act_hi = sb("act_hi", [P, KT, SEQ], F32R)
        act_lo = sb("act_lo", [P, KT, SEQ], F32R)
        merged = sb("merged", [P, TB, D_MODEL])
        gates = sb("gates", [P, TB, 2, N])
        heads_a = sb("heads_a", [P, TB, 8, HD])
        heads_b = sb("heads_b", [P, TB, 6, HD])
        heads_c = sb("heads_c", [P, TB, 1, HD])
        roped_a = sb("roped_a", [P, TB, 8, HD])
        roped_b = sb("roped_b", [P, TB, 8, HD])
        roped_c = sb("roped_c", [P, TB, 2, HD])
        rope_t = sb("rope_t", [P, 8, HD])
        qk_t = sb("qk_t", [P, 12, SEQ])
        v_b = sb("v_b", [P, TB, 2 * HD])
        v_c = sb("v_c", [P, TB, HD])
        lat = sb("lat", [P, TB, P])
        lat_t = sb("lat_t", [P, SEQ])
        idx_w = sb("idx_w", [P, TB, 4])
        sq = sb("sq", [P, TB, N])
        junk = sb("junk", [P, 256])
        logits = sb("logits", [P, 4, SEQ])
        probs = sb("probs", [P, 4, SEQ])
        probs_t = sb("probs_t", [P, TB, 4, P])
        top8 = sb("top8", [P, 8])
        row = sb("row", [P, 8, 4])
        za = probs_t[:].rearrange("p t h q -> p t (h q)")
        zd = roped_b[:, 0].rearrange("p (t h) d -> p t (h d)", t=TB)
        mixed = roped_b[:, 1].rearrange("p (a h) d -> p a (h d)", a=2)
        mask_b = sb("mask_b", [P, P + SEQ])
        mask_c = sb("mask_c", [P, P + SEQ])
        pool_a = sb("pool_a", [P, 4, SEQ])
        pool_b = sb("pool_b", [P, 4, P])
        spatial_t = sb("spatial_t", [P, A_GROUPS, P])
        y_ac_hi = sb("y_ac_hi", [P, 2, SEQ], F32R)
        y_ac_lo = sb("y_ac_lo", [P, 2, SEQ], F32R)
        y_d_hi = sb("y_d_hi", [P, 2, SEQ], F32R)
        y_d_lo = sb("y_d_lo", [P, 2, SEQ], F32R)
        y_h_hi = sb("y_h_hi", [P, 4, SEQ], F32R)
        y_h_lo = sb("y_h_lo", [P, 4, SEQ], F32R)
        ms = sb("ms", [P, len(NORMS), 8])
        rstd = sb("rstd", [P, len(NORMS), 8])
        ss = sb("ss", [P, len(NORMS), 8])
        ffn_scale = sb("ffn_scale", [P, TB])
        rs_half = sb("rs_half", [P, 2, TB])
        minus_half = sb("minus_half", [P, 8])
        ident = sb("ident", [P, P])
        inv_freq = sb("inv_freq", [P, HD // 2])
        pos_i = sb("pos_i", [P, TB], I32)
        pos_f = sb("pos_f", [P, TB])
        cos_t = sb("cos_t", [P, TB, 2, HD // 2])
        sin_t = sb("sin_t", [P, TB, 2, HD // 2])
        g_mix = sb("g_mix", [P, KT])
        g_ffn = sb("g_ffn", [P, KT])
        g_v = sb("g_v", [P, A_WIDTH])
        g_head = sb("g_head", [P, 4, HD])
        g_lat = sb("g_lat", [P, P])
        sinks = sb("sinks", [P, 8])
        b_sp = sb("b_sp", [P, A_GROUPS])
        w_sp = sb("w_sp", [P, A_GROUPS, P])
        w_grp = sb("w_grp", [P, 2, HD])
        s_grp = sb("s_grp", [P, 2])
        w_ukv = sb("w_ukv", [P, 2, HD])

        big = ctx.enter_context(nc.psum_tensor("big", [P, 4, N], F32))
        mix = ctx.enter_context(nc.psum_tensor("mix", [P, 4, N], F32))

        early = []

        def signal(name, per_layer):
            return Signal(sem(name), per_layer)

        def signal_from_1(name, per_layer):
            early.append(Signal(sem(name), per_layer, 1))
            return early[-1]

        landed = [signal(f"landed{s}", 16 * sum(dmas_of(u) for u in UNITS[s::RAW])) for s in range(RAW)]
        params_in = signal("params_in", 16 * N_PARAMS)
        x_in = sem("x_in")
        pos_in = sem("pos_in")
        hi_ready = signal("hi_ready", NU)
        lo_by_dve = signal_from_1("lo_by_dve", len(DVE_UNITS))
        lo_by_pool = signal("lo_by_pool", len(POOL_UNITS))
        split_free = signal("split_free", NU)
        main_full = [signal(f"main_full{b}", MAIN_PER[b]) for b in range(4)]
        main_drained = [signal_from_1(f"main_drained{b}", MAIN_PER[b]) for b in range(4)]
        mix_full = [signal(f"mix_full{b}", MIX_PER[b]) for b in range(4)]
        mix_drained = [signal_from_1(f"mix_drained{b}", MIX_PER[b]) for b in range(4)]
        squares = {n: signal(f"squares_{n}", 1 if n[0] in "KQ" else 2) for n in NORMS}
        ms_ready = signal("ms_ready", len(NORMS))
        rstd_ready = signal("rstd_ready", len(NORMS))
        scales_ready = signal("scales_ready", 2)
        act_hi_ready = signal("act_hi_ready", 12)
        act_lo_ready = signal_from_1("act_lo_ready", 8)
        lat_normed = signal("lat_normed", 1)
        wt_masked = signal("wt_masked", 1)
        roped = {n: signal(f"roped_{n}", 1) for n in "IKQC"}
        za_squared = signal("za_squared", 2)
        gelu_arg = signal("gelu_arg", 2)
        gelu_tanh = signal("gelu_tanh", 2)
        gelu_ready = signal("gelu_ready", 2)
        v_normed = signal("v_normed", 1)
        ya_ready = signal("ya_ready", 1)
        y_hi = signal("y_hi", 2 + len(ATTN))
        indexed = signal("indexed", 2)
        merge_product = signal("merge_product", 16)
        row_max = signal("row_max", len(ATTN))
        exp_ready = signal("exp_ready", len(ATTN))
        probs_ready = signal("probs_ready", len(ATTN))
        merged_ready = signal("merged_ready", 4)
        ffn_tanh = signal("ffn_tanh", 2 * NF)
        hid_hi = signal("hid_hi", 2 * NF)
        dve_step = signal("dve_step", DVE_STEPS)
        const_pool = sem("const_pool")
        const_dve = sem("const_dve")
        const_sin = sem("const_sin")
        stored = sem("stored")
        alone_dve, alone_pe, alone_sp = sem("alone_dve"), sem("alone_pe"), sem("alone_sp")

        def main_bank(*use):
            return MAIN[use][0]

        def mix_bank(*use):
            return MIX[use][0]

        def main_is_full(l, *use):
            bank, n = MAIN[use]
            return main_full[bank].nth(l, n + 1)

        def main_is_drained(l, *use):
            bank, n = MAIN[use]
            return main_drained[bank].nth(l, n + 1)

        def main_is_free(l, *use):
            bank, n = MAIN[use]
            return main_drained[bank].nth(l, n)

        def mix_is_full(l, *use):
            bank, n = MIX[use]
            return mix_full[bank].nth(l, n + 1)

        def mix_is_drained(l, *use):
            bank, n = MIX[use]
            return mix_drained[bank].nth(l, n + 1)

        def mix_is_free(l, *use):
            bank, n = MIX[use]
            return mix_drained[bank].nth(l, n)

        def unit_landed(l, u):
            s = u % RAW
            return landed[s].nth(l, 16 * sum(dmas_of(q) for q in UNITS[s:u + 1:RAW]))

        def low_part(l, u):
            if u in POOL_UNITS:
                return lo_by_pool.nth(l, POOL_UNITS.index(u) + 1)
            return lo_by_dve.nth(l, DVE_UNITS.index(u) + 1)

        def unit_cols(u):
            return UNITS[u][2] if UNITS[u][0] == "in" else N

        def splits_in(slot):
            if slot == FIRST["wo", 0]:
                return [slot + 2, slot + 3]
            if slot == FIRST["wo", 0] + 1:
                return []
            return [slot + 2] if slot + 2 < NU else []

        def tok(tb):
            return slice(tb * P, (tb + 1) * P)

        def keys(tb):
            return P * (tb + 1)

        def mask_cols(tb):
            return slice(0, P) if tb == 0 else slice(P, P + SEQ)

        def score_view(bank, tb):
            return mix[:, bank, 0:2 * keys(tb)].rearrange("p (h k) -> p h k", h=2)

        def by4(bank):
            return bank.rearrange("p (k n) -> p k n", k=4)

        def over_tokens(col):
            return col.unsqueeze(2).to_broadcast([P, col.shape[1], P])

        OUT_SLOT = {}
        for b in BRANCHES:
            for c in range(2):
                for tb in range(TB):
                    OUT_SLOT[b, c, tb] = FIRST["out", b] if OUT_K[b] == 2 else FIRST["out", b, c]
        WO = FIRST["wo", 0]
        DN = {f: FIRST["dn", f] for f in range(NF)}
        HID_AT = {0: FIRST["gu", 1], 1: FIRST["gu", 2], **{f: DN[f - 2] for f in range(2, NF)}}
        EVICT_AT = {0: FIRST["gu", 2], **{f: DN[f - 1] for f in range(1, NF)}}

        Y = {"A": (y_ac_hi, y_ac_lo), "C": (y_ac_hi, y_ac_lo), "D": (y_d_hi, y_d_lo), "B": (y_h_hi, y_h_lo)}
        HEADS = {"I": (heads_a, roped_a), "K": (heads_b, roped_b), "Q": (heads_a, roped_a),
                 "C": (heads_c, roped_c)}
        angle = [logits[:, r, 0:HD].rearrange("p (t k) -> p t k", t=TB) for r in range(4)]
        more = [probs[:, r, 0:HD].rearrange("p (t k) -> p t k", t=TB) for r in range(4)]

        block = ctx.enter_context(nc.Block())

        @block.sync
        def _(sp):
            sp.dma_start(xs[:], x[0].rearrange("(t p) d -> p t d", p=P)).then_inc(x_in, 16)
            sp.dma_start(pos_i[:], positions[0].rearrange("(t p) -> p t", p=P),
                         allow_slow_non_contiguous=True).then_inc(pos_in, 16)

            def load_unit(l, u):
                kind, a, b, h = UNITS[u]
                s = u % RAW
                if u < RAW:
                    sp.wait_ge(*lo_by_dve.nth(l, 0)).then_inc(alone_sp, 1)
                else:
                    sp.wait_ge(*low_part(l, u - RAW)).then_inc(alone_sp, 1)
                rows = slice(h * PIECES * P, (h + 1) * PIECES * P)
                dst = raw[:, s]
                if kind == "in":
                    sp.dma_start(dst[:, :, 0:b], w_in[l, rows, a:a + b].rearrange("(k p) n -> p k n", p=P)
                                 ).then_inc(landed[s].sem, 16)
                elif kind == "out2":
                    sp.dma_start(dst.rearrange("p (k c) n -> p k (c n)", k=2),
                                 w_out[a][l].rearrange("(k p) n -> p k n", p=P)).then_inc(landed[s].sem, 16)
                elif kind == "out4":
                    sp.dma_start(dst, w_out[a][l, :, b * N:(b + 1) * N].rearrange("(k p) n -> p k n", p=P)
                                 ).then_inc(landed[s].sem, 16)
                elif kind == "wo":
                    sp.dma_start(dst, w_o[l, rows, a * N:(a + 1) * N].rearrange("(k p) n -> p k n", p=P)
                                 ).then_inc(landed[s].sem, 16)
                elif kind == "gu":
                    for half in range(2):
                        c0 = half * FFN + a * FC
                        sp.dma_start(dst[:, :, half * FC:(half + 1) * FC],
                                     w_gate_up[l, rows, c0:c0 + FC].rearrange("(k p) n -> p k n", p=P)
                                     ).then_inc(landed[s].sem, 16)
                else:
                    sp.dma_start(dst.rearrange("p (k c) n -> p k (c n)", k=2),
                                 w_down[l, a * FC:(a + 1) * FC, :].rearrange("(k p) n -> p k n", p=P)
                                 ).then_inc(landed[s].sem, 16)

            def load_params(l):
                sp.wait_ge(*act_lo_ready.nth(l, 0))
                params = (
                    (g_mix[:], norm_mix[l].rearrange("(k p) -> p k", p=P)),
                    (g_ffn[:], norm_ffn[l].rearrange("(k p) -> p k", p=P)),
                    (g_lat[:], c_latent_gain[l].partition_broadcast(P)),
                    (g_head[:, 0], b_q_gain[l].partition_broadcast(P)),
                    (g_head[:, 1], b_k_gain[l].partition_broadcast(P)),
                    (g_head[:, 2], c_q_gain[l].partition_broadcast(P)),
                    (g_head[:, 3], c_k_gain[l].partition_broadcast(P)),
                    (w_sp[:], a_w_spatial[l].rearrange("g i j -> i g j")),
                    (w_ukv[:, 0], c_w_uk[l]),
                    (w_ukv[:, 1], c_w_uv[l]),
                    (g_v[:], a_v_gain[l].partition_broadcast(P)),
                    (sinks[:], b_sinks[l].partition_broadcast(P)),
                    (w_grp[:], d_w_group[l].rearrange("(a b) c d -> (b c) a d", b=2)),
                    (s_grp[:], d_scale[l].rearrange("(a p) -> p a", p=P)),
                    (b_sp[:], a_b_spatial[l].rearrange("g i -> i g")),
                )
                assert len(params) == N_PARAMS
                for dst, src in params:
                    sp.dma_start(dst, src, allow_slow_non_contiguous=True).then_inc(params_in.sem, 16)

            with sp.Fori(0, DEPTH) as l:
                load_unit(l, 0)
                load_unit(l, 1)
                load_params(l)
                for u in range(2, NU):
                    load_unit(l, u)
            for b in range(4):
                sp.wait_ge(*main_drained[b].nth(DEPTH, 0))
            sp.dma_start(out[0].rearrange("(t p) d -> p t d", p=P), xs[:]).then_inc(stored, 16)
            sp.wait_ge(stored, 16)

        @block.gpsimd
        def _(pool):
            for s in range(SPLIT - 1):
                nc.gpsimd.memset(top8[:, s:s + 1], 0.0).then_inc(split_free.sem, 1)
            for k, signal_ in enumerate(early):
                nc.gpsimd.memset(junk[:, k:k + 1], 0.0).then_inc(signal_.sem, 1)
            nc.gpsimd.memset(minus_half[:], -0.5).then_inc(const_pool, 1)
            nc.gpsimd.memset(ident[:], 0.0).then_inc(const_pool, 1)
            for k in range(HD // 2):
                f = float(np.float32(ROPE_THETA ** (-2.0 * k / HD)))
                nc.gpsimd.memset(inv_freq[:, k:k + 1], f).then_inc(const_pool, 1)
            done = 2 + HD // 2
            pool.wait_ge(const_pool, done)
            nc.gpsimd.affine_select(out=ident[:], in_=ident[:], compare_op=ALU.not_equal, fill=1.0, base=0,
                                    pattern=[[-1, P]], channel_multiplier=1).then_inc(const_pool, 1)
            for g, w in enumerate(D_POOLS):
                nc.gpsimd.memset(pool_a[:, g, :], 1.0 / w).then_inc(const_pool, 1)
                nc.gpsimd.memset(pool_b[:, g, :], 1.0 / w).then_inc(const_pool, 1)
            done += 1 + 2 * len(D_POOLS)
            pool.wait_ge(const_pool, done)
            starts = [(g, t) for g, w in enumerate(D_POOLS) for t in range(w - 1)]
            for g, t in starts:
                nc.gpsimd.memset(pool_a[:, g, t:t + 1], float(np.float32(1.0) / np.float32(t + 1))
                                 ).then_inc(const_pool, 1)
            done += len(starts)
            pool.wait_ge(const_pool, done)
            for sign in (1, -1):
                for g, w in enumerate(D_POOLS):
                    for tile, width in ((pool_a, SEQ), (pool_b, P)):
                        nc.gpsimd.affine_select(out=tile[:, g, :], in_=tile[:, g, :], compare_op=ALU.is_ge,
                                                fill=0.0, base=0 if sign == 1 else w - 1,
                                                pattern=[[sign, width]], channel_multiplier=-sign
                                                ).then_inc(const_pool, 1)
                done += 2 * len(D_POOLS)
                pool.wait_ge(const_pool, done)
            assert done == POOL_CONSTS

            def split(l, u):
                pool.wait_ge(*hi_ready.nth(l, u + 1))
                n = unit_cols(u)
                nc.gpsimd.tensor_tensor(w_lo[:, u % SPLIT, :, 0:n], raw[:, u % RAW, :, 0:n],
                                        w_hi[:, u % SPLIT, :, 0:n].bitcast(F32), ALU.subtract
                                        ).then_inc(lo_by_pool.sem, 1)

            def power(l, name):
                i = NORMS.index(name)
                pool.wait_ge(*ms_ready.nth(l, i + 1))
                w = NORM_WIDTH[name]
                nc.gpsimd.tensor_tensor(rstd[:, i, 0:w], ms[:, i, 0:w], minus_half[:, 0:w], ALU.pow
                                        ).then_inc(rstd_ready.sem, 1)

            with pool.Fori(0, DEPTH) as l:
                for u in POOL_UNITS:
                    for name in NORMS:
                        if POWER_BEFORE[name] == u:
                            power(l, name)
                    split(l, u)
                power(l, "ffn")

        @block.scalar
        def _(act):
            act.wait_ge(const_dve, DVE_ANGLES)
            nc.scalar.activation(sin_t[:, :, 1, :], angle[2], ACT.Sin).then_inc(const_sin, 1)
            nc.scalar.activation(cos_t[:, :, 0, :], more[2], ACT.Sin).then_inc(const_sin, 1)

            def split(l, u):
                n = unit_cols(u)
                act.wait_ge(*unit_landed(l, u))
                act.wait_ge(*split_free.nth(l, u + 1))
                nc.scalar.activation(w_hi[:, u % SPLIT, :, 0:n], raw[:, u % RAW, :, 0:n], ACT.Copy
                                     ).then_inc(hi_ready.sem, 1)

            def sum_squares(name, col, src, dst):
                nc.scalar.activation(dst, src, ACT.Square, accum_out=ss[:, NORMS.index(name), col:col + 1]
                                     ).then_inc(squares[name].sem, 1)

            def x_squares(l, name, tb):
                if name == "ffn":
                    for c in range(2):
                        act.wait_ge(*main_is_drained(l, "wo", c, tb))
                else:
                    for c in range(2):
                        act.wait_ge(*main_drained[main_bank("dn", c, tb)].nth(l, 0))
                spare = (logits, probs)[tb]
                sum_squares(name, tb, xs[:, tb, :], spare[:].rearrange("p h k -> p (h k)"))

            def high_gained(l, stage, tb):
                for h in range(2):
                    act.wait_ge(*mix_is_drained(l, stage, tb, h))
                    nc.scalar.activation(act_hi[:, 4 * h:4 * h + 4, tok(tb)], by4(sq[:, h, :]), ACT.Copy
                                         ).then_inc(act_hi_ready.sem, 1)

            def high_merged(l, tb):
                for h in range(2):
                    act.wait_ge(*mix_is_full(l, "mT", tb, h))
                    nc.scalar.activation(act_hi[:, 4 * h:4 * h + 4, tok(tb)],
                                         by4(mix[:, mix_bank("mT", tb, h), :]), ACT.Copy, scale=0.5
                                         ).then_inc(act_hi_ready.sem, 1)

            def project_out(l, name, tb):
                bank = main_bank("proj", name, tb)
                z = big[:, bank, :]
                r = rstd[:, NORMS.index("mix"), tb:tb + 1]
                drained = main_drained[bank].sem
                act.wait_ge(*main_is_full(l, "proj", name, tb))
                if name == "idx":
                    if tb == 0:
                        act.wait_ge(*rstd_ready.nth(l, NORMS.index("mix") + 1))
                    nc.scalar.activation(lat[:, tb, :], z[:, 0:P], ACT.Copy, scale=r)
                    nc.scalar.activation(heads_a[:, tb, 0:5, :],
                                         z[:, P:P + 5 * HD].rearrange("p (h d) -> p h d", d=HD), ACT.Copy,
                                         scale=r)
                    nc.scalar.activation(idx_w[:, tb, :], z[:, P + 5 * HD:P + 5 * HD + 4], ACT.Copy, scale=r
                                         ).then_inc(drained, 1)
                    act.wait_ge(*main_is_drained(l, "proj", name, tb))
                    sum_squares("lat", tb, lat[:, tb, :], junk[:, tok(tb)])
                elif name == "kv":
                    nc.scalar.activation(heads_b[:, tb, 0:2, :],
                                         z[:, 0:P].rearrange("p (h d) -> p h d", d=HD), ACT.Copy, scale=r)
                    nc.scalar.activation(v_b[:, tb, :], z[:, P:2 * P], ACT.Copy, scale=r)
                    nc.scalar.activation(heads_b[:, tb, 2:6, :],
                                         z[:, 2 * P:4 * P].rearrange("p (h d) -> p h d", d=HD), ACT.Copy,
                                         scale=r).then_inc(drained, 1)
                    act.wait_ge(*main_is_drained(l, "proj", name, tb))
                    nc.scalar.activation(sq[:, tb, 0:6 * HD],
                                         heads_b[:, tb].rearrange("p h d -> p (h d)"), ACT.Square
                                         ).then_inc(squares[f"K{tb}"].sem, 1)
                elif name == "bq":
                    act.wait_ge(*mix_is_full(l, "TI", 1))
                    nc.scalar.activation(heads_a[:, tb, :, :], z.rearrange("p (h d) -> p h d", d=HD),
                                         ACT.Copy, scale=r).then_inc(drained, 1)
                    act.wait_ge(*main_is_drained(l, "proj", name, tb))
                    act.wait_ge(*ms_ready.nth(l, NORMS.index(f"K{tb}") + 1))
                    nc.scalar.activation(sq[:, tb, :], heads_a[:, tb].rearrange("p h d -> p (h d)"), ACT.Square
                                         ).then_inc(squares[f"Q{tb}"].sem, 1)
                elif name == "za":
                    nc.scalar.activation(za[:, tb, :], z, ACT.Copy, scale=r).then_inc(drained, 1)
                    act.wait_ge(*main_is_drained(l, "proj", name, tb))
                    nc.scalar.activation(merged[:, tb, 0:N], za[:, tb, :], ACT.Square,
                                         scale=float(np.sqrt(GELU_A))).then_inc(za_squared.sem, 1)
                else:
                    nc.scalar.activation(zd[:, tb, :], z[:, 0:256], ACT.Copy, scale=r).then_inc(drained, 1)

            def drain(l, dst, *use, src=None, func=ACT.Copy, scale=1.0):
                act.wait_ge(*mix_is_full(l, *use))
                nc.scalar.activation(dst, mix[:, mix_bank(*use), :] if src is None else src, func, scale=scale
                                     ).then_inc(mix_drained[mix_bank(*use)].sem, 1)

            def drain_pairs(l, name, first, banks, last_cols=N):
                for k in range(banks):
                    n = last_cols if k == banks - 1 else N
                    drain(l, qk_t[:, first + 2 * k:first + 2 * k + n // SEQ, :], *((name, k) if name != "TC" else (name,)),
                          src=mix[:, mix_bank(*((name, k) if name != "TC" else (name,))), 0:n].rearrange("p (a t) -> p a t", t=SEQ))

            def gate_tanh(l, b, c, tb):
                bank = main_bank("gate", b, c, tb)
                act.wait_ge(*main_is_full(l, "gate", b, c, tb))
                if b != BRANCHES[0]:
                    last = BRANCHES[BRANCHES.index(b) - 1]
                    act.wait_ge(*main_is_drained(l, "out", last, c, tb))
                elif c == 0 and tb == 0:
                    act.wait_ge(*scales_ready.nth(l, 1))
                nc.scalar.activation(gates[:, tb, c, :], big[:, bank, :], ACT.Tanh, scale=rs_half[:, 0, tb:tb + 1]
                                     ).then_inc(main_drained[bank].sem, 1)

            def exps(l, i):
                _, _, tb = ATTN[i]
                act.wait_ge(*row_max.nth(l, i + 1))
                if i > 0:
                    act.wait_ge(*mix_is_full(l, "T", i - 1, ATTN[i - 1][2]))
                if ATTN[i][0] == "B":
                    nc.scalar.activation(row[:, 3, :], row[:, 2, :], ACT.Exp)
                for h in range(4):
                    e = nc.scalar.activation(probs[:, h, 0:keys(tb)], logits[:, h, 0:keys(tb)], ACT.Exp,
                                             scale=SCALE, bias=row[:, 1, h:h + 1], accum_out=row[:, 4, h:h + 1])
                e.then_inc(exp_ready.sem, 1)

            def y_high(l, dst, scale, *use, n=None):
                act.wait_ge(*mix_is_full(l, *use))
                src = mix[:, mix_bank(*use), :] if n is None else mix[:, mix_bank(*use), 0:n]
                return nc.scalar.activation(dst, src.rearrange("p (k t) -> p k t", k=2), ACT.Copy, scale=scale)

            def steps(l, s):
                for j, (name, _, _) in enumerate(PROJ):
                    for tb in range(TB):
                        if s == 2 * j + tb + 1:
                            project_out(l, name, tb)
                if s == PE_AT["wT"]:
                    drain(l, spatial_t[:], "wT", src=by4(mix[:, mix_bank("wT"), :]))
                if s == PE_AT["latT"]:
                    drain(l, lat_t[:], "latT", src=mix[:, mix_bank("latT"), 0:SEQ])
                if s == PE_AT["TI"]:
                    drain_pairs(l, "TI", 0, 2, SEQ)
                if s == PE_AT["kv"]:
                    kv = mix[:, mix_bank("kv"), 0:2 * P].rearrange("p (t v d) -> p t v d", t=TB, v=2)
                    act.wait_ge(*mix_is_full(l, "kv"))
                    nc.scalar.activation(heads_c[:, :, 0, :], kv[:, :, 0, :], ACT.Copy)
                    drain(l, v_c[:], "kv", src=kv[:, :, 1, :])
                    act.wait_ge(*mix_is_drained(l, "kv"))
                    act.wait_ge(*squares["lat"].nth(l, 2))
                    for tb in range(TB):
                        sum_squares("ck", tb, heads_c[:, tb, 0, :], junk[:, tb * HD:(tb + 1) * HD])
                for tb in range(TB):
                    if s == PE_AT[f"idx{tb}"]:
                        if tb == 1:
                            act.wait_ge(*indexed.nth(l, 1))
                        for odd in range(2):
                            drain(l, logits[:, odd::2, 0:keys(tb)], "idx", tb, odd,
                                  src=score_view(mix_bank("idx", tb, odd), tb), func=ACT.Relu, scale=SCALE * 0.5)
                if s == PE_AT["TK"]:
                    drain_pairs(l, "TK", 7, 2)
                for tb in range(TB):
                    if s == 9 + tb:
                        act.wait_ge(*gelu_arg.nth(l, tb + 1))
                        nc.scalar.activation(merged[:, tb, 0:N], merged[:, tb, N:2 * N], ACT.Tanh, scale=GELU_C
                                             ).then_inc(gelu_tanh.sem, 1)
                if s == 11:
                    for tb in range(TB):
                        act.wait_ge(*gelu_ready.nth(l, tb + 1))
                        act.wait_ge(*(squares["ck"].nth(l, 2) if tb == 0 else squares["v"].nth(l, 1)))
                        sum_squares("v", tb, za[:, tb, A_WIDTH:], junk[:])
                if s == PE_AT["TQ"]:
                    drain_pairs(l, "TQ", 3, 2)
                    drain_pairs(l, "TC", 11, 1, SEQ)
                for b in BRANCHES:
                    for c in range(2):
                        for tb in range(TB):
                            if s == FIRST["gate", b, c] + tb + 1:
                                gate_tanh(l, b, c, tb)
                if s == PE_AT["mixed"]:
                    drain(l, mixed[:], "mixed", src=mix[:, mix_bank("mixed"), :].rearrange("p (a t) -> p a t", a=2))
                if s == PE_AT["yaT"]:
                    y_high(l, y_ac_hi[:], 0.5, "yaT").then_inc(y_hi.sem, 1)
                if s == PE_AT["ydT"]:
                    for odd in range(2):
                        part = slice(HD * odd, HD * odd + HD)
                        act.wait_ge(*mix_is_full(l, "ydT", odd))
                        for a in range(2):
                            e = nc.scalar.activation(y_d_hi[part, a, :],
                                                     mix[part, mix_bank("ydT", odd), a * SEQ:(a + 1) * SEQ],
                                                     ACT.Copy, scale=s_grp[part, a:a + 1])
                    e.then_inc(y_hi.sem, 1)
                for i, (m, kv, tb) in enumerate(ATTN):
                    if s == T_AT[i]:
                        for k in range(tb + 1):
                            drain(l, probs_t[:, k], "T", i, k, src=by4(mix[:, mix_bank("T", i, k), :]))
                    if s == Y_AT[i]:
                        if i == 4:
                            act.wait_ge(*main_is_full(l, "out", "A", 1, 1))
                        hi, k0 = Y[m][0], 2 * kv if m == "B" else 0
                        y_high(l, hi[:, k0:k0 + 2, tok(tb)], 1.0, "Y", i, n=2 * P).then_inc(y_hi.sem, 1)
                if s == WO:
                    high_merged(l, 0)
                if s == WO + 3:
                    high_gained(l, "h2T", 0)
                    x_squares(l, "ffn", 0)
                if s == WO + 4:
                    high_gained(l, "h2T", 1)
                    x_squares(l, "ffn", 1)
                for f in range(NF):
                    if s == EVICT_AT[f]:
                        for tb in range(TB):
                            act.wait_ge(*mix_is_full(l, "hid", f, tb))
                            nc.scalar.activation(y_h_hi[:, 2 * (f % 2):2 * (f % 2) + 2, tok(tb)],
                                                 mix[:, mix_bank("hid", f, tb), 0:FC].rearrange("p (k t) -> p k t", k=2),
                                                 ACT.Copy).then_inc(hid_hi.sem, 1)
                    if s == HID_AT[f]:
                        for tb in range(TB):
                            if f == 0 and tb == 0:
                                act.wait_ge(*scales_ready.nth(l, 2))
                            act.wait_ge(*mix_is_full(l, "gu", f, tb))
                            if f >= 2:
                                act.wait_ge(*mix_is_drained(l, "gu", f - 2, tb))
                            nc.scalar.activation(gates[:, tb, 0, FC * (f % 2):FC * (f % 2) + FC],
                                                 mix[:, mix_bank("gu", f, tb), 0:FC], ACT.Tanh,
                                                 scale=rs_half[:, 1, tb:tb + 1]).then_inc(ffn_tanh.sem, 1)

            act.wait_ge(x_in, 16)
            with act.Fori(0, DEPTH) as l:
                split(l, 0)
                split(l, 1)
                high_gained(l, "hT", 0)
                x_squares(l, "mix", 0)
                x_squares(l, "mix", 1)
                high_gained(l, "hT", 1)
                for s in range(NU):
                    steps(l, s)
                    for u in splits_in(s):
                        split(l, u)
                        if s == WO and u == WO + 2:
                            high_merged(l, 1)
                    for i in range(len(ATTN)):
                        if s == S_AT[i]:
                            exps(l, i)

        @block.vector
        def _(dve):
            H = P // 2
            nc.vector.memset(mask_b[:], 0.0).then_inc(const_dve, 1)
            dve.wait_ge(const_dve, 1)
            nc.vector.memset(mask_b[0:H, H:P], NEG).then_inc(const_dve, 1)
            nc.vector.memset(mask_b[0:H, P:P + CHUNK], NEG).then_inc(const_dve, 1)
            nc.vector.memset(mask_b[0:H, P + 3 * CHUNK:P + 4 * CHUNK], NEG).then_inc(const_dve, 1)
            nc.vector.memset(mask_b[H:P, P:P + 2 * CHUNK], NEG).then_inc(const_dve, 1)
            dve.wait_ge(pos_in, 16)
            nc.vector.tensor_copy(pos_f[:], pos_i[:]).then_inc(const_dve, 1)
            dve.wait_ge(const_dve, 6)
            dve.wait_ge(const_pool, 2 + HD // 2)
            for tb in range(TB):
                nc.vector.tensor_scalar(angle[0][:, tb, :], inv_freq[:], pos_f[:, tb:tb + 1], None, ALU.mult
                                        ).then_inc(const_dve, 1)
            dve.wait_ge(const_dve, 8)
            done = 8
            for turn, buf in ((0.0, angle), (0.25, more)):
                nc.vector.tensor_scalar(buf[1], angle[0], 1.0 / (2 * np.pi), turn, ALU.mult, ALU.add
                                        ).then_inc(const_dve, 1)
                dve.wait_ge(const_dve, done + 1)
                nc.vector.tensor_scalar(buf[1], buf[1], ROUNDER, None, ALU.add).then_inc(const_dve, 1)
                dve.wait_ge(const_dve, done + 2)
                nc.vector.tensor_scalar(buf[1], buf[1], ROUNDER, None, ALU.subtract).then_inc(const_dve, 1)
                dve.wait_ge(const_dve, done + 3)
                done += 3
                at = angle[0]
                for part in TWO_PI:
                    nc.vector.scalar_tensor_tensor(out=buf[2], in0=buf[1], scalar=-part, in1=at,
                                                   op0=ALU.mult, op1=ALU.add).then_inc(const_dve, 1)
                    done += 1
                    dve.wait_ge(const_dve, done)
                    at = buf[2]
                nc.vector.tensor_scalar(buf[2], buf[2], float(np.float32(turn * 2 * np.pi)), None, ALU.add
                                        ).then_inc(const_dve, 1)
                dve.wait_ge(const_dve, done + 1)
                nc.vector.tensor_scalar(buf[2], buf[2], 3.1415925, -3.1415925, ALU.min, ALU.max
                                        ).then_inc(const_dve, 1)
                done += 2
                dve.wait_ge(const_dve, done)
            assert done == DVE_ANGLES
            dve.wait_ge(const_sin, 2)
            nc.vector.tensor_scalar(sin_t[:, :, 0, :], sin_t[:, :, 1, :], -1.0, None, ALU.mult
                                    ).then_inc(const_dve, 1)
            nc.vector.tensor_copy(cos_t[:, :, 1, :], cos_t[:, :, 0, :]).then_inc(const_dve, 1)
            dve.wait_ge(const_pool, POOL_CONSTS)
            for g in range(len(D_POOLS)):
                nc.vector.tensor_tensor(pool_a[:, g, 0:P], pool_a[:, g, 0:P], ident[:], ALU.subtract
                                        ).then_inc(const_dve, 1)
                nc.vector.tensor_tensor(pool_b[:, g, :], pool_b[:, g, :], ident[:], ALU.subtract
                                        ).then_inc(const_dve, 1)
            dve.wait_ge(const_dve, DVE_CONSTS)

            count = [0]

            def step(l, ins, alone=False):
                ins.then_inc(dve_step.sem, 1)
                count[0] += 1
                w = dve.wait_ge(*dve_step.nth(l, count[0]))
                if alone:
                    w.then_inc(alone_dve, 1)

            def split(l, u):
                n = unit_cols(u)
                dve.wait_ge(*hi_ready.nth(l, u + 1))
                nc.vector.tensor_tensor(w_lo[:, u % SPLIT, :, 0:n], raw[:, u % RAW, :, 0:n],
                                        w_hi[:, u % SPLIT, :, 0:n].bitcast(F32), ALU.subtract
                                        ).then_inc(lo_by_dve.sem, 1)

            def gained(l, stage, tb):
                gain, base = (g_mix, 0) if stage == "hT" else (g_ffn, 4)
                for h in range(2):
                    dve.wait_ge(*mix_is_full(l, stage, tb, h))
                    if tb == 1:
                        dve.wait_ge(*act_lo_ready.nth(l, base + h + 1))
                    bank = mix_bank(stage, tb, h)
                    nc.vector.tensor_tensor(by4(sq[:, h, :]), by4(mix[:, bank, :]),
                                            over_tokens(gain[:, 4 * h:4 * h + 4]), ALU.mult
                                            ).then_inc(mix_drained[bank].sem, 1)
                for h in range(2):
                    dve.wait_ge(*act_hi_ready.nth(l, (0 if stage == "hT" else 8) + 2 * tb + h + 1))
                    nc.vector.tensor_tensor(act_lo[:, 4 * h:4 * h + 4, tok(tb)], by4(sq[:, h, :]),
                                            act_hi[:, 4 * h:4 * h + 4, tok(tb)].bitcast(F32), ALU.subtract
                                            ).then_inc(act_lo_ready.sem, 1)

            def merged_low(l, tb):
                for h in range(2):
                    bank = mix_bank("mT", tb, h)
                    dve.wait_ge(*act_hi_ready.nth(l, 4 + 2 * tb + h + 1))
                    nc.vector.scalar_tensor_tensor(out=act_lo[:, 4 * h:4 * h + 4, tok(tb)], in0=by4(mix[:, bank, :]),
                                                   scalar=0.5, in1=act_hi[:, 4 * h:4 * h + 4, tok(tb)].bitcast(F32),
                                                   op0=ALU.mult, op1=ALU.subtract
                                                   ).then_inc(mix_drained[bank].sem, 1)

            def mean_square(l, name, src, width):
                nc.vector.tensor_scalar(ms[:, NORMS.index(name), 0:NORM_WIDTH[name]], src, 1.0 / width, EPS,
                                        ALU.mult, ALU.add).then_inc(ms_ready.sem, 1)

            def mean_of_sums(l, name, width):
                dve.wait_ge(*squares[name].nth(l, 2))
                mean_square(l, name, ss[:, NORMS.index(name), 0:2], width)

            def norm_factor(l, name):
                dve.wait_ge(*rstd_ready.nth(l, NORMS.index(name) + 1))
                return rstd[:, NORMS.index(name), :]

            def scales(l, name, j):
                r = norm_factor(l, name)
                nc.vector.tensor_scalar(rs_half[:, j, :], r[:, 0:TB], 0.5, None, ALU.mult
                                        ).then_inc(scales_ready.sem, 1)

            def head_squares(l, name, heads):
                tb = int(name[1])
                dve.wait_ge(*squares[name].nth(l, 1))
                i = NORMS.index(name)
                step(l, nc.vector.tensor_reduce(ss[:, i, 0:heads],
                                                sq[:, tb, 0:heads * HD].rearrange("p (h d) -> p h d", d=HD),
                                                AX_X, ALU.add))
                mean_square(l, name, ss[:, i, 0:heads], HD)

            def norm_heads(l, name, tile, tb, gains):
                heads = tile.shape[2]
                v = tile[:, tb]
                step(l, nc.vector.tensor_tensor(v, v, norm_factor(l, name)[:, 0:heads].unsqueeze(2)
                                                .to_broadcast([P, heads, HD]), ALU.mult))
                for h0, h1, g in gains:
                    last = nc.vector.tensor_tensor(tile[:, tb, h0:h1], tile[:, tb, h0:h1],
                                                   g_head[:, g:g + 1, :].to_broadcast([P, h1 - h0, HD]), ALU.mult)
                step(l, last)

            def rope(l, kind, tile, out_tile, tb, heads, places, last):
                v = tile[:, tb, 0:heads]
                half = HD // 2
                c = cos_t[:, tb].rearrange("p a k -> p (a k)").unsqueeze(1).to_broadcast([P, heads, HD])
                s0 = sin_t[:, tb, 0:1, :].to_broadcast([P, heads, half])
                s1 = sin_t[:, tb, 1:2, :].to_broadcast([P, heads, half])
                nc.vector.tensor_tensor(rope_t[:, 0:heads, 0:half], v[:, :, half:], s0, ALU.mult)
                step(l, nc.vector.tensor_tensor(rope_t[:, 0:heads, half:], v[:, :, 0:half], s1, ALU.mult))
                step(l, nc.vector.tensor_tensor(v, v, c, ALU.mult))
                for n, (h0, h1, copies, at) in enumerate(places):
                    for k in range(copies):
                        dst = out_tile[:, tb, at + k:at + k + copies * (h1 - h0 - 1) + 1:copies, :]
                        ins = nc.vector.tensor_tensor(dst, tile[:, tb, h0:h1], rope_t[:, h0:h1], ALU.add)
                if last:
                    ins.then_inc(roped[kind].sem, 1)
                    dve.wait_ge(*roped[kind].nth(l, 1))
                else:
                    step(l, ins)

            def index_scores(l, tb):
                n = keys(tb)
                cols = mask_cols(tb)
                acc = mask_c[:, cols]
                for odd in range(2):
                    dve.wait_ge(*mix_is_drained(l, "idx", tb, odd))
                step(l, nc.vector.tensor_scalar(acc, logits[:, 0, 0:n], idx_w[:, tb, 0:1], None, ALU.mult))
                for h in range(1, 4):
                    ins = nc.vector.scalar_tensor_tensor(out=acc, in0=logits[:, h, 0:n], scalar=idx_w[:, tb, h:h + 1],
                                                         in1=acc, op0=ALU.mult, op1=ALU.add)
                    if h < 3:
                        step(l, ins)
                ins.then_inc(indexed.sem, 1)
                dve.wait_ge(*indexed.nth(l, tb + 1))
                step(l, nc.vector.memset(mask_c[0:CHUNK, cols.stop - CHUNK:cols.stop], OUTSIDE), alone=True)

            def top_k(l, tb, rounds):
                acc = mask_c[:, mask_cols(tb)]
                for _ in rounds:
                    step(l, nc.vector.max(top8[:], acc), alone=True)
                    step(l, nc.vector.match_replace(acc, top8[:], acc, TAKEN), alone=True)
                if rounds.stop == TOPK // 8:
                    step(l, nc.vector.tensor_scalar(acc, acc, TAKEN, NEG, ALU.not_equal, ALU.mult))

            def gelu_args(l, tb):
                dve.wait_ge(*za_squared.nth(l, tb + 1))
                nc.vector.scalar_tensor_tensor(out=merged[:, tb, N:2 * N], in0=merged[:, tb, 0:N], scalar=1.0,
                                               in1=za[:, tb, :], op0=ALU.add, op1=ALU.mult
                                               ).then_inc(gelu_arg.sem, 1)

            def gelu_end(l, tb):
                dve.wait_ge(*gelu_tanh.nth(l, tb + 1))
                nc.vector.scalar_tensor_tensor(out=za[:, tb, :], in0=merged[:, tb, 0:N], scalar=1.0,
                                               in1=za[:, tb, :], op0=ALU.add, op1=ALU.mult
                                               ).then_inc(gelu_ready.sem, 1)

            def v_norm(l):
                r = norm_factor(l, "v")
                step(l, nc.vector.tensor_scalar(rstd[:, NORMS.index("v"), 2:4], r[:, 0:2], 0.5, None, ALU.mult))
                for tb in range(TB):
                    ins = nc.vector.scalar_tensor_tensor(out=merged[:, tb, N:N + A_WIDTH], in0=za[:, tb, A_WIDTH:],
                                                         scalar=rstd[:, NORMS.index("v"), 2 + tb:3 + tb], in1=g_v[:],
                                                         op0=ALU.mult, op1=ALU.mult)
                ins.then_inc(v_normed.sem, 1)

            def gated(l):
                dve.wait_ge(*mix_is_full(l, "spatial"))
                bank = mix_bank("spatial")
                for g in range(A_GROUPS):
                    cols = slice(g * HD, (g + 1) * HD)
                    s_g = mix[:, bank, :].rearrange("p (t c) -> p t c", t=TB)[:, :, cols]
                    ins = nc.vector.scalar_tensor_tensor(
                        out=za[:, :, A_WIDTH + g * HD:A_WIDTH + (g + 1) * HD], in0=s_g, scalar=b_sp[:, g:g + 1],
                        in1=za[:, :, cols], op0=ALU.add, op1=ALU.mult)
                ins.then_inc(mix_drained[bank].sem, 1)

            def softmax_in(l, i):
                m, kv, tb = ATTN[i]
                mask = mask_b if m == "B" else mask_c
                for odd in range(2):
                    bank = mix_bank("S", i, odd)
                    dve.wait_ge(*mix_is_full(l, "S", i, odd))
                    nc.vector.tensor_tensor(logits[:, odd::2, 0:keys(tb)], score_view(bank, tb),
                                            mask[:, mask_cols(tb)].unsqueeze(1).to_broadcast([P, 2, keys(tb)]),
                                            ALU.add).then_inc(mix_drained[bank].sem, 1)
                for odd in range(2):
                    dve.wait_ge(*mix_is_drained(l, "S", i, odd))
                step(l, nc.vector.tensor_reduce(row[:, 0, :], logits[:, :, 0:keys(tb)], AX_X, ALU.max))
                if m == "B":
                    sink = sinks[:, 4 * kv:4 * kv + 4]
                    step(l, nc.vector.scalar_tensor_tensor(out=row[:, 0, :], in0=row[:, 0, :], scalar=SCALE, in1=sink,
                                                           op0=ALU.mult, op1=ALU.max))
                    step(l, nc.vector.tensor_tensor(row[:, 2, :], sink, row[:, 0, :], ALU.subtract))
                    nc.vector.tensor_scalar(row[:, 1, :], row[:, 0, :], -1.0, None, ALU.mult
                                            ).then_inc(row_max.sem, 1)
                else:
                    nc.vector.tensor_scalar(row[:, 1, :], row[:, 0, :], -SCALE, None, ALU.mult
                                            ).then_inc(row_max.sem, 1)

            def softmax_out(l, i):
                m, kv, tb = ATTN[i]
                dve.wait_ge(*exp_ready.nth(l, i + 1))
                total = row[:, 4, :]
                if m == "B":
                    step(l, nc.vector.tensor_tensor(row[:, 5, :], total, row[:, 3, :], ALU.add))
                    total = row[:, 5, :]
                step(l, nc.vector.reciprocal(row[:, 6, :], total))
                p = probs[:, :, 0:keys(tb)]
                nc.vector.tensor_tensor(p, p, row[:, 6, :].unsqueeze(2).to_broadcast([P, 4, keys(tb)]), ALU.mult
                                        ).then_inc(probs_ready.sem, 1)

            def y_low(l, n, hi, lo, scale, *use, cols=N):
                bank = mix_bank(*use)
                dve.wait_ge(*y_hi.nth(l, n))
                nc.vector.scalar_tensor_tensor(out=lo, in0=mix[:, bank, 0:cols].rearrange("p (k t) -> p k t", k=2),
                                               scalar=scale, in1=hi.bitcast(F32), op0=ALU.mult, op1=ALU.subtract
                                               ).then_inc(mix_drained[bank].sem, 1)

            def merge(l, b, c, tb):
                bank = main_bank("out", b, c, tb)
                dst = merged[:, tb, c * N:(c + 1) * N]
                dve.wait_ge(*main_is_full(l, "out", b, c, tb))
                dve.wait_ge(*main_is_drained(l, "gate", b, c, tb))
                t = dst if b == BRANCHES[0] else gates[:, tb, c, :]
                nc.vector.scalar_tensor_tensor(out=t, in0=gates[:, tb, c, :], scalar=1.0, in1=big[:, bank, :],
                                               op0=ALU.add, op1=ALU.mult).then_inc(merge_product.sem, 1)
                merges[0] += 1
                dve.wait_ge(*merge_product.nth(l, merges[0]))
                if b == BRANCHES[0]:
                    nc.vector.memset(row[:, 7, 0:1], 0.0).then_inc(main_drained[bank].sem, 1)
                    return
                nc.vector.tensor_tensor(dst, dst, t, ALU.add).then_inc(main_drained[bank].sem, 1)

            merges = [0]

            def add_residual(l, *use):
                _, c, tb = use
                bank = main_bank(*use)
                dst = xs[:, tb, c * N:(c + 1) * N]
                dve.wait_ge(*main_is_full(l, *use))
                nc.vector.tensor_tensor(dst, big[:, bank, :], dst, ALU.add).then_inc(main_drained[bank].sem, 1)

            def hidden(l, f, tb):
                bank = mix_bank("gu", f, tb)
                cols = slice(FC * (f % 2), FC * (f % 2) + FC)
                h = gates[:, tb, 1, cols]
                dve.wait_ge(*ffn_tanh.nth(l, 2 * f + tb + 1))
                if f >= 2:
                    dve.wait_ge(*mix_is_full(l, "hid", f - 2, tb))
                step(l, nc.vector.scalar_tensor_tensor(out=h, in0=gates[:, tb, 0, cols], scalar=1.0,
                                                       in1=mix[:, bank, 0:FC], op0=ALU.add, op1=ALU.mult))
                nc.vector.scalar_tensor_tensor(out=h, in0=h, scalar=ffn_scale[:, tb:tb + 1], in1=mix[:, bank, FC:2 * FC],
                                               op0=ALU.mult, op1=ALU.mult).then_inc(mix_drained[bank].sem, 1)

            def hidden_low(l, f, tb):
                bank = mix_bank("hid", f, tb)
                k = slice(2 * (f % 2), 2 * (f % 2) + 2)
                dve.wait_ge(*hid_hi.nth(l, 2 * f + tb + 1))
                nc.vector.tensor_tensor(y_h_lo[:, k, tok(tb)], mix[:, bank, 0:FC].rearrange("p (k t) -> p k t", k=2),
                                        y_h_hi[:, k, tok(tb)].bitcast(F32), ALU.subtract
                                        ).then_inc(mix_drained[bank].sem, 1)

            def steps(l, s):
                for b in BRANCHES:
                    order = [(c, tb) for tb in range(TB) for c in range(2)] if OUT_K[b] == 2 else \
                            [(c, tb) for c in range(2) for tb in range(TB)]
                    for c, tb in order:
                        if s == OUT_SLOT[b, c, tb] + 1 and not (b == BRANCHES[-1]):
                            merge(l, b, c, tb)
                if s == 1:
                    scales(l, "mix", 0)
                for tb in range(TB):
                    if s == 2 + tb:
                        dve.wait_ge(*main_is_drained(l, "proj", "idx", tb))
                        rope(l, "I", heads_a, roped_a, tb, 5, [(0, 4, 1, 0), (4, 5, 2, 4)], tb == 1)
                if s == 2:
                    mean_of_sums(l, "lat", P)
                if s == 3:
                    r = norm_factor(l, "lat")
                    for tb in range(TB):
                        ins = nc.vector.scalar_tensor_tensor(out=lat[:, tb, :], in0=lat[:, tb, :], scalar=r[:, tb:tb + 1],
                                                             in1=g_lat[:], op0=ALU.mult, op1=ALU.mult)
                    ins.then_inc(lat_normed.sem, 1)
                if s == PE_AT["wT"] + 1:
                    dve.wait_ge(*mix_is_drained(l, "wT"))
                    nc.vector.memset(spatial_t[CHUNK:P, :, 0:CHUNK], 0.0).then_inc(wt_masked.sem, 1)
                for tb in range(TB):
                    if s == 4 + tb:
                        head_squares(l, f"K{tb}", 6)
                    if s == 5 + tb:
                        norm_heads(l, f"K{tb}", heads_b, tb, [(0, 2, 1), (2, 6, 2)])
                        rope(l, "K", heads_b, roped_b, tb, 6, [(0, 2, 2, 0), (2, 6, 1, 4)], tb == 1)
                    if s == 6 + tb:
                        head_squares(l, f"Q{tb}", 8)
                    if s == (7, 9)[tb]:
                        norm_heads(l, f"Q{tb}", heads_a, tb, [(0, 8, 0)])
                        rope(l, "Q", heads_a, roped_a, tb, 8, [(0, 8, 1, 0)], tb == 1)
                if s == 8:
                    mean_of_sums(l, "ck", HD)
                for tb in range(TB):
                    if s == PE_AT[f"idx{tb}"]:
                        index_scores(l, tb)
                    if s == 8 + tb:
                        gelu_args(l, tb)
                    if s == 10 + tb - (1 if tb else 0):
                        gelu_end(l, tb)
                if s == 10:
                    r = norm_factor(l, "ck")
                    for tb in range(TB):
                        ins = nc.vector.scalar_tensor_tensor(out=heads_c[:, tb, 0, :], in0=heads_c[:, tb, 0, :],
                                                             scalar=r[:, tb:tb + 1], in1=g_head[:, 3, :],
                                                             op0=ALU.mult, op1=ALU.mult)
                    step(l, ins)
                    for tb in range(TB):
                        rope(l, "C", heads_c, roped_c, tb, 1, [(0, 1, 2, 0)], tb == 1)
                if s == 11:
                    mean_of_sums(l, "v", 4 * A_WIDTH)
                    v_norm(l)
                if s == PE_AT["spatial"]:
                    gated(l)
                if s == PE_AT["yaT"]:
                    y_low(l, 1, y_ac_hi[:], y_ac_lo[:], 0.5, "yaT")
                if s == PE_AT["ydT"]:
                    dve.wait_ge(*y_hi.nth(l, 2))
                    for odd in range(2):
                        part = slice(HD * odd, HD * odd + HD)
                        bank = mix_bank("ydT", odd)
                        for a in range(2):
                            ins = nc.vector.scalar_tensor_tensor(
                                out=y_d_lo[part, a, :], in0=mix[part, bank, a * SEQ:(a + 1) * SEQ],
                                scalar=s_grp[part, a:a + 1], in1=y_d_hi[part, a, :].bitcast(F32),
                                op0=ALU.mult, op1=ALU.subtract)
                        ins.then_inc(mix_drained[bank].sem, 1)
                for i, (m, kv, tb) in enumerate(ATTN):
                    if s == T_AT[i] - 1:
                        softmax_out(l, i)
                for i, (m, kv, tb) in enumerate(ATTN):
                    if s == Y_AT[i]:
                        k0 = 2 * kv if m == "B" else 0
                        hi, lo = Y[m]
                        y_low(l, 3 + i, hi[:, k0:k0 + 2, tok(tb)], lo[:, k0:k0 + 2, tok(tb)], 1.0, "Y", i, cols=2 * P)
                    if s == S_AT[i]:
                        softmax_in(l, i)
                if s == WO:
                    for tb in range(TB):
                        for c in range(2):
                            merge(l, BRANCHES[-1], c, tb)
                        if tb == 0:
                            merged_low(l, 0)
                if s == WO + 3:
                    add_residual(l, "wo", 0, 0)
                    add_residual(l, "wo", 1, 0)
                    gained(l, "h2T", 0)
                    add_residual(l, "wo", 0, 1)
                if s == WO + 4:
                    add_residual(l, "wo", 1, 1)
                    gained(l, "h2T", 1)
                if s == WO + 5:
                    mean_of_sums(l, "ffn", D_MODEL)
                    scales(l, "ffn", 1)
                    dve.wait_ge(*scales_ready.nth(l, 2))
                    step(l, nc.vector.tensor_tensor(ffn_scale[:], rs_half[:, 1, :],
                                                    rstd[:, NORMS.index("ffn"), 0:TB], ALU.mult))
                for f in range(NF):
                    if s == EVICT_AT[f]:
                        for tb in range(TB):
                            hidden_low(l, f, tb)
                    if s == HID_AT[f]:
                        for tb in range(TB):
                            hidden(l, f, tb)

            with dve.Fori(0, DEPTH) as l:
                dve.wait_ge(*params_in.nth(l, params_in.per_layer))
                gained(l, "hT", 0)
                mean_of_sums(l, "mix", D_MODEL)
                gained(l, "hT", 1)
                for s in range(NU):
                    steps(l, s)
                    for u in splits_in(s):
                        if u in DVE_UNITS:
                            split(l, u)
                        if s == WO and u == WO + 2:
                            merged_low(l, 1)
                    if s in TOPK_AT:
                        tb, a, b = TOPK_AT[s]
                        top_k(l, tb, range(a, b))
                for tb in range(TB):
                    for c in range(2):
                        add_residual(l, "dn", c, tb)
            assert count[0] == DVE_STEPS, count[0]

        @block.tensor
        def _(pe):
            def segment(l, use, parts, tb, hi, lo, releases, first=True, last=True):
                bank = main_bank(*use) if use in MAIN else None
                if bank is not None:
                    dst, full = big[:, bank, :], main_full[bank].sem
                    if first:
                        pe.wait_ge(*main_is_free(l, *use))
                else:
                    bank = mix_bank(*use)
                    dst, full = mix[:, bank, :], mix_full[bank].sem
                    if first:
                        pe.wait_ge(*mix_is_free(l, *use))
                seen = set()
                for n, (u, piece, k) in enumerate(parts):
                    if u not in seen:
                        pe.wait_ge(*low_part(l, u))
                        seen.add(u)
                    w = unit_cols(u)
                    xh, xl = hi[:, k, tok(tb)], lo[:, k, tok(tb)]
                    wh, wl = w_hi[:, u % SPLIT, piece, 0:w], w_lo[:, u % SPLIT, piece, 0:w]
                    end = last and n == len(parts) - 1
                    ins = nc.tensor.matmul(dst[:, 0:w], xh, wh, start=first and n == 0, stop=False)
                    if n == 0 and -1 in releases:
                        ins.then_inc(split_free.sem, 1)
                    nc.tensor.matmul(dst[:, 0:w], xh, wl, start=False, stop=False)
                    ins = nc.tensor.matmul(dst[:, 0:w], xl, wh, start=False, stop=end)
                    if end:
                        ins.then_inc(full, 1)
                    elif n in releases:
                        ins.then_inc(split_free.sem, 1)

            def turn(l, stage, tb):
                src = merged if stage == "mT" else xs
                for h in range(2):
                    bank = mix_bank(stage, tb, h)
                    if stage == "mT":
                        pe.wait_ge(*main_is_drained(l, "out", BRANCHES[-1], h, tb))
                    elif stage == "h2T":
                        pe.wait_ge(*main_is_drained(l, "wo", h, tb))
                    else:
                        pe.wait_ge(*main_drained[main_bank("dn", h, tb)].nth(l, 0))
                    pe.wait_ge(*mix_is_free(l, stage, tb, h))
                    for j in range(4):
                        k = 4 * h + j
                        ins = nc.tensor.transpose(mix[:, bank, j * P:(j + 1) * P], src[:, tb, k * P:(k + 1) * P],
                                                  ident[:])
                        if stage == "hT" and tb == 0 and k == 0:
                            ins.then_inc(split_free.sem, 1)
                    ins.then_inc(mix_full[bank].sem, 1)

            def turn_pairs(l, name, first, tile, pairs):
                for k in range((pairs + 1) // 2):
                    use = (name, k) if name != "TC" else (name,)
                    bank = mix_bank(*use)
                    pe.wait_ge(*mix_is_free(l, *use))
                    for p in range(2 * k, min(2 * k + 2, pairs)):
                        for tb in range(TB):
                            ins = nc.tensor.transpose(
                                mix[:, bank, (p % 2) * SEQ + tb * P:(p % 2) * SEQ + (tb + 1) * P],
                                tile[:, tb, 2 * p:2 * p + 2, :].rearrange("p h d -> p (h d)"), ident[:])
                    ins.then_inc(mix_full[bank].sem, 1)

            def scores(l, uses, tb, q_pair, k_pair):
                for odd in range(2):
                    use = (*uses, odd)
                    bank = mix_bank(*use)
                    half = slice(HD * odd, HD * odd + HD)
                    pe.wait_ge(*mix_is_free(l, *use))
                    for a in range(2):
                        ins = nc.tensor.matmul(score_view(bank, tb)[:, a, :], qk_t[half, q_pair + a, tok(tb)],
                                               qk_t[half, k_pair, 0:keys(tb)], start=True, stop=True)
                    ins.then_inc(mix_full[bank].sem, 1)

            def attention(l, s):
                for i, (m, kv, tb) in enumerate(ATTN):
                    if s == Y_AT[i]:
                        bank = mix_bank("Y", i)
                        for k in range(tb + 1):
                            pe.wait_ge(*mix_is_drained(l, "T", i, k))
                        for odd in range(2):
                            for k in range(tb + 1):
                                v = v_b[:, k, kv * HD:(kv + 1) * HD] if m == "B" else v_c[:, k, :]
                                ins = nc.tensor.matmul(
                                    mix[HD * odd:HD * odd + HD, bank, 0:2 * P].rearrange("p (a t) -> p a t", a=2), v,
                                    probs_t[:, k].rearrange("p (a b) t -> p a b t", b=2)[:, :, odd, :],
                                    start=(k == 0), stop=(k == tb))
                        ins.then_inc(mix_full[bank].sem, 1)
                for i, (m, kv, tb) in enumerate(ATTN):
                    if s == S_AT[i]:
                        scores(l, ("S", i), tb, 3 + 2 * kv if m == "B" else 9, 7 + kv if m == "B" else 11)
                for i, (m, kv, tb) in enumerate(ATTN):
                    if s == T_AT[i]:
                        pe.wait_ge(*probs_ready.nth(l, i + 1))
                        for k in range(tb + 1):
                            bank = mix_bank("T", i, k)
                            pe.wait_ge(*mix_is_free(l, "T", i, k))
                            for h in range(4):
                                ins = nc.tensor.transpose(mix[:, bank, h * P:(h + 1) * P],
                                                          probs[:, h, k * P:(k + 1) * P], ident[:])
                            ins.then_inc(mix_full[bank].sem, 1)

            def steps(l, s):
                if s == PE_AT["wT"]:
                    bank = mix_bank("wT")
                    pe.wait_ge(*mix_is_free(l, "wT"))
                    for g in range(A_GROUPS):
                        ins = nc.tensor.transpose(mix[:, bank, g * P:(g + 1) * P], w_sp[:, g, :], ident[:])
                    ins.then_inc(mix_full[bank].sem, 1)
                if s == PE_AT["latT"]:
                    bank = mix_bank("latT")
                    pe.wait_ge(*lat_normed.nth(l, 1))
                    pe.wait_ge(*mix_is_free(l, "latT"))
                    for tb in range(TB):
                        ins = nc.tensor.transpose(mix[:, bank, tb * P:(tb + 1) * P], lat[:, tb, :], ident[:])
                    ins.then_inc(mix_full[bank].sem, 1)
                if s == PE_AT["TI"]:
                    pe.wait_ge(*roped["I"].nth(l, 1))
                    turn_pairs(l, "TI", 0, roped_a, 3)
                if s == PE_AT["kv"]:
                    bank = mix_bank("kv")
                    pe.wait_ge(*mix_is_drained(l, "latT"))
                    pe.wait_ge(*mix_is_free(l, "kv"))
                    for tb in range(TB):
                        ins = nc.tensor.matmul(mix[:, bank, tb * P:(tb + 1) * P], lat_t[:, tok(tb)],
                                               w_ukv[:].rearrange("p a d -> p (a d)"), start=True, stop=True)
                    ins.then_inc(mix_full[bank].sem, 1)
                for tb in range(TB):
                    if s == PE_AT[f"idx{tb}"]:
                        for k in range(2):
                            pe.wait_ge(*mix_is_drained(l, "TI", k))
                        scores(l, ("idx", tb), tb, 0, 2)
                if s == PE_AT["TK"]:
                    pe.wait_ge(*roped["K"].nth(l, 1))
                    turn_pairs(l, "TK", 7, roped_b, 4)
                if s == PE_AT["TQ"]:
                    pe.wait_ge(*roped["Q"].nth(l, 1))
                    turn_pairs(l, "TQ", 3, roped_a, 4)
                    pe.wait_ge(*roped["C"].nth(l, 1))
                    turn_pairs(l, "TC", 11, roped_c, 1)
                if s == PE_AT["spatial"]:
                    bank = mix_bank("spatial")
                    pe.wait_ge(*wt_masked.nth(l, 1))
                    pe.wait_ge(*v_normed.nth(l, 1))
                    pe.wait_ge(*mix_is_free(l, "spatial"))
                    for tb in range(TB):
                        for g in range(A_GROUPS):
                            cols = slice(tb * A_WIDTH + g * HD, tb * A_WIDTH + (g + 1) * HD)
                            ins = nc.tensor.matmul(mix[:, bank, cols], spatial_t[:, g, :],
                                                   merged[:, tb, N + g * HD:N + (g + 1) * HD], start=True, stop=True)
                    ins.then_inc(mix_full[bank].sem, 1)
                if s == PE_AT["mixed"]:
                    bank = mix_bank("mixed")
                    for tb in range(TB):
                        pe.wait_ge(*main_is_drained(l, "proj", "zd", tb))
                    pe.wait_ge(*mix_is_free(l, "mixed"))
                    for g in range(4):
                        part = slice(HD * (g % 2), HD * (g % 2) + HD)
                        c0 = (g // 2) * SEQ
                        nc.tensor.matmul(mix[part, bank, c0:c0 + SEQ], zd[:, 0, g * HD:(g + 1) * HD], pool_a[:, g, :],
                                         start=True, stop=False)
                        ins = nc.tensor.matmul(mix[part, bank, c0 + P:c0 + SEQ], zd[:, 1, g * HD:(g + 1) * HD],
                                               pool_b[:, g, :], start=False, stop=True)
                    ins.then_inc(mix_full[bank].sem, 1)
                if s == PE_AT["yaT"]:
                    bank = mix_bank("yaT")
                    pe.wait_ge(*mix_is_drained(l, "spatial"))
                    pe.wait_ge(*mix_is_free(l, "yaT"))
                    for k in range(2):
                        for tb in range(TB):
                            ins = nc.tensor.transpose(mix[:, bank, k * SEQ + tb * P:k * SEQ + (tb + 1) * P],
                                                      za[:, tb, A_WIDTH + k * P:A_WIDTH + (k + 1) * P], ident[:])
                    ins.then_inc(mix_full[bank].sem, 1)
                if s == PE_AT["ydT"]:
                    pe.wait_ge(*mix_is_drained(l, "mixed"))
                    for odd in range(2):
                        part = slice(HD * odd, HD * odd + HD)
                        bank = mix_bank("ydT", odd)
                        pe.wait_ge(*mix_is_free(l, "ydT", odd)).then_inc(alone_pe, 1)
                        for a in range(2):
                            ins = nc.tensor.matmul(mix[part, bank, a * SEQ:(a + 1) * SEQ], w_grp[part, a, :],
                                                   mixed[part, a, :], start=True, stop=True)
                        ins.then_inc(mix_full[bank].sem, 1)
                attention(l, s)

            def chunk(l, use, unit, tb, carried):
                parts = [(unit + h, piece, 4 * h + piece) for h in range(2) for piece in range(PIECES)]
                segment(l, (*use, tb), parts, tb, act_hi, act_lo,
                        ({-1} if tb == 0 and carried else set()) | ({PIECES - 1} if tb == 1 else set()))

            pe.wait_ge(x_in, 16)
            pe.wait_ge(const_dve, DVE_CONSTS)
            pe.wait_ge(const_pool, POOL_CONSTS)
            with pe.Fori(0, DEPTH) as l:
                turn(l, "hT", 0)
                turn(l, "hT", 1)
                for j, (name, _, _) in enumerate(PROJ):
                    for tb in range(TB):
                        steps(l, 2 * j + tb)
                        if j == 0:
                            pe.wait_ge(*act_lo_ready.nth(l, 2 * tb + 2))
                        chunk(l, ("proj", name), 2 * j, tb, j > 0)
                for b in BRANCHES:
                    for c in range(2):
                        unit = FIRST["gate", b, c]
                        for tb in range(TB):
                            steps(l, unit + tb)
                            chunk(l, ("gate", b, c), unit, tb, True)
                    hi, lo = Y[b]
                    if OUT_K[b] == 2:
                        unit = FIRST["out", b]
                        steps(l, unit)
                        if b == "A":
                            pe.wait_ge(*mix_is_drained(l, "yaT"))
                        elif b == "D":
                            for odd in range(2):
                                pe.wait_ge(*mix_is_drained(l, "ydT", odd))
                        else:
                            pe.wait_ge(*mix_is_drained(l, "Y", 5))
                        for tb in range(TB):
                            for c in range(2):
                                segment(l, ("out", b, c, tb), [(unit, 2 * k + c, k) for k in range(2)], tb, hi, lo,
                                        {-1} if (tb, c) == (0, 0) else set())
                    else:
                        for c in range(2):
                            unit = FIRST["out", b, c]
                            steps(l, unit)
                            if c == 0:
                                pe.wait_ge(*mix_is_drained(l, "Y", 3))
                            for tb in range(TB):
                                segment(l, ("out", b, c, tb), [(unit, k, k) for k in range(4)], tb, hi, lo,
                                        {-1} if tb == 0 else set())
                u0 = FIRST["wo", 0]

                def wo(l, c, tb):
                    parts = [(u0 + 2 * c + h, piece, 4 * h + piece) for h in range(2) for piece in range(PIECES)]
                    releases = {(0, 0): {-1}, (0, 1): set(), (1, 0): {PIECES - 1}, (1, 1): {-1, PIECES - 1}}[tb, c]
                    segment(l, ("wo", c, tb), parts, tb, act_hi, act_lo, releases)

                turn(l, "mT", 0)
                for h in range(2):
                    pe.wait_ge(*mix_is_drained(l, "mT", 0, h))
                wo(l, 0, 0)
                turn(l, "mT", 1)
                wo(l, 1, 0)
                for h in range(2):
                    pe.wait_ge(*mix_is_drained(l, "mT", 1, h))
                wo(l, 0, 1)
                turn(l, "h2T", 0)
                wo(l, 1, 1)

                def gate_up(l, f, tb, halves=(0, 1)):
                    unit = FIRST["gu", f]
                    for h in halves:
                        parts = [(unit + h, piece, 4 * h + piece) for piece in range(PIECES)]
                        releases = set()
                        if tb == 0 and h == 0 and f in (0, 1, 2):
                            releases = {-1}
                        if tb == 1 and h == 0:
                            releases = {PIECES - 1}
                        segment(l, ("gu", f, tb), parts, tb, act_hi, act_lo, releases, first=h == 0, last=h == 1)

                def turn_hidden(l, f):
                    for tb in range(TB):
                        bank = mix_bank("hid", f, tb)
                        pe.wait_ge(*mix_is_drained(l, "gu", f, tb))
                        for k in range(2):
                            c0 = FC * (f % 2) + k * P
                            ins = nc.tensor.transpose(mix[:, bank, k * P:(k + 1) * P], gates[:, tb, 1, c0:c0 + P],
                                                      ident[:])
                        ins.then_inc(mix_full[bank].sem, 1)

                def down(l, f):
                    unit = FIRST["dn", f]
                    for tb in range(TB):
                        pe.wait_ge(*mix_is_drained(l, "hid", f, tb))
                        for c in range(2):
                            releases = set()
                            if (tb, c) == (0, 0) and f < NF - 2:
                                releases = {-1}
                            if (tb, c) == (1, 1) and f < NF - 1:
                                releases = releases | {1}
                            parts = [(unit, 2 * k + c, 2 * (f % 2) + k) for k in range(2)]
                            segment(l, ("dn", c, tb), parts, tb, y_h_hi, y_h_lo, releases, first=f == 0,
                                    last=f == NF - 1)

                for h in range(2):
                    pe.wait_ge(*act_lo_ready.nth(l, 4 + h + 1))
                gate_up(l, 0, 0, (0,))
                turn(l, "h2T", 1)
                gate_up(l, 0, 0, (1,))
                for h in range(2):
                    pe.wait_ge(*act_lo_ready.nth(l, 6 + h + 1))
                gate_up(l, 0, 1)
                for f in range(1, NF):
                    gate_up(l, f, 0)
                    gate_up(l, f, 1)
                    turn_hidden(l, f - 1)
                    if f >= 2:
                        down(l, f - 2)
                turn_hidden(l, NF - 1)
                down(l, NF - 2)
                down(l, NF - 1)


_INS = ['x', 'positions', 'norm_mix', 'w_in', 'a_v_gain', 'a_w_spatial', 'a_b_spatial', 'a_w_out',
        'b_q_gain', 'b_k_gain', 'b_sinks', 'b_w_out', 'c_q_gain', 'c_k_gain', 'c_latent_gain',
        'c_w_uk', 'c_w_uv', 'c_w_out', 'd_w_group', 'd_scale', 'd_w_out', 'w_o', 'norm_ffn',
        'w_gate_up', 'w_down']


def kernel(**inputs):
    import concourse.bacc as bacc
    from concourse.bass_utils import run_bass_kernel_spmd

    nc = bacc.Bacc("TRN2", target_bir_lowering=False, num_devices=1)
    arrays, args = {}, []
    for name in _INS:
        a = np.ascontiguousarray(inputs[name])
        arrays[f"in_{name}"] = a
        args.append(nc.dram_tensor(f"in_{name}", a.shape, mybir.dt.from_np(a.dtype), kind="ExternalInput").ap())
    args.append(nc.dram_tensor("out_y", (1, SEQ, D_MODEL), F32, kind="ExternalOutput").ap())
    trunk_kernel(nc, *args)
    r = run_bass_kernel_spmd(nc, [arrays], core_ids=[0])
    return r.results[0]["out_y"]
```
